# Optimizing a Trainium2 kernel written in Bass

```python
import jax
import jax.numpy as jnp
from jax import lax
import numpy as np

D_MODEL = 1024
BATCH = 1
SEQ = 256
DEPTH = 2
DEC_BATCH = 1
DEC_SEQ = 512
PAST_LEN = 128

GRID_W = 64
N_MIXERS = 2
EXPAND = 2
BRANCH_WIDTH = EXPAND * D_MODEL
SSD_HEAD_DIM = 64
SSD_HEADS = BRANCH_WIDTH // SSD_HEAD_DIM
SSD_GROUPS = 4
SSD_STATE = 128
SSD_CONV = 5
SSD_CHUNK = 128
SSD_CONV_DIM = BRANCH_WIDTH + 2 * SSD_GROUPS * SSD_STATE
NA_HEAD_DIM = 64
NA_HEADS = BRANCH_WIDTH // NA_HEAD_DIM
NA_KH = 8
NA_KW = 16
MEM_TOKENS = 256
MEM_HEADS = 4
MEM_HEAD_DIM = D_MODEL // MEM_HEADS
MEM_WIDTH = MEM_HEADS * MEM_HEAD_DIM
MIX_WIDTH = BRANCH_WIDTH + MEM_WIDTH
SSD_IN = MIX_WIDTH + SSD_CONV_DIM + 2 * SSD_HEADS + MEM_WIDTH
NA_IN = MIX_WIDTH + 3 * BRANCH_WIDTH + MEM_WIDTH
N_SSD_LAYERS = (DEPTH + 1) // 2
N_NA_LAYERS = DEPTH // 2
EPS = 1e-6

kernel_name = 'hybrid_ssd_natten_memory_encoder'

def rmsnorm(x, g):
    xf = x.astype(jnp.float32)
    y = xf * lax.rsqrt(jnp.mean(xf * xf, axis=-1, keepdims=True) + EPS)
    return (y * g.astype(jnp.float32)).astype(x.dtype)

def depthwise_conv_centred(u, w, b):
    pad = SSD_CONV // 2
    y = lax.conv_general_dilated(u, w[:, None, :].astype(u.dtype), window_strides=(1,),
                                 padding=[(pad, pad)], dimension_numbers=('NWC', 'WIO', 'NWC'),
                                 feature_group_count=u.shape[-1])
    return y + b.astype(u.dtype)

def ssd_chunked(x, a_dt, bm, cm):
    b, t, _, p = x.shape
    c, l = t // SSD_CHUNK, SSD_CHUNK
    r = SSD_HEADS // SSD_GROUPS
    x = x.reshape(b, c, l, SSD_GROUPS, r, p)
    bm = bm.reshape(b, c, l, SSD_GROUPS, SSD_STATE)
    cm = cm.reshape(b, c, l, SSD_GROUPS, SSD_STATE)
    a = a_dt.reshape(b, c, l, SSD_GROUPS, r).transpose(0, 1, 3, 4, 2)
    a_cs = jnp.cumsum(a, axis=-1)
    lower = jnp.tril(jnp.ones((l, l), dtype=bool))
    seg = a_cs[..., :, None] - a_cs[..., None, :]
    decay_ls = jnp.exp(jnp.where(lower, seg, -jnp.inf))
    cb = jnp.einsum('bclgn,bcsgn->bcgls', cm, bm)
    y_diag = jnp.einsum('bcgrls,bcsgrp->bclgrp', cb[:, :, :, None] * decay_ls, x)
    decay_to_end = jnp.exp(a_cs[..., -1:] - a_cs)
    states = jnp.einsum('bclgn,bcgrl,bclgrp->bcgrpn', bm, decay_to_end, x)
    chunk_decay = jnp.exp(a_cs[..., -1])

    def step(carry, inp):
        st, dec = inp
        return carry * dec[..., None, None] + st, carry

    init = jnp.zeros(states.shape[:1] + states.shape[2:], states.dtype)
    _, prev = lax.scan(step, init, (states.swapaxes(0, 1), chunk_decay.swapaxes(0, 1)))
    prev = prev.swapaxes(0, 1)
    y_off = jnp.einsum('bclgn,bcgrpn,bcgrl->bclgrp', cm, prev, jnp.exp(a_cs))
    return (y_diag + y_off).reshape(b, t, SSD_HEADS, p)

def ssd_direction(xs, bm, cm, dt_raw, dt_bias, a_log):
    dt = jax.nn.softplus(dt_raw.astype(jnp.float32) + dt_bias.astype(jnp.float32))
    a_dt = -jnp.exp(a_log.astype(jnp.float32)) * dt
    return ssd_chunked(xs * dt[..., None].astype(xs.dtype), a_dt, bm, cm)

def memory_attention(q_mem, mem_n, w_mem_kv):
    b, t, _ = q_mem.shape
    m = mem_n.shape[1]
    q = q_mem.reshape(b, t, MEM_HEADS, MEM_HEAD_DIM) * (MEM_HEAD_DIM ** -0.5)
    kv = (mem_n @ w_mem_kv).reshape(b, m, 2, MEM_HEADS, MEM_HEAD_DIM)
    k, v = kv[:, :, 0], kv[:, :, 1]
    s = jnp.einsum('bthd,bmhd->bhtm', q, k).astype(jnp.float32)
    p = jax.nn.softmax(s, axis=-1).astype(v.dtype)
    return jnp.einsum('bhtm,bmhd->bthd', p, v).reshape(b, t, MEM_WIDTH)

def neighbourhood_attention(q, k, v, rpb):
    b, t, h, dh = q.shape
    rows = t // GRID_W
    kh = min(NA_KH, rows)
    qg = q.reshape(b, rows, GRID_W, h, dh) * (dh ** -0.5)
    kg = k.reshape(b, rows, GRID_W, h, dh)
    vg = v.reshape(b, rows, GRID_W, h, dh)
    col = jnp.arange(GRID_W)
    col_start = jnp.clip(col - NA_KW // 2, 0, GRID_W - NA_KW)
    col_in = (col[None, :] >= col_start[:, None]) & (col[None, :] < col_start[:, None] + NA_KW)
    dc = jnp.clip(col[None, :] - col[:, None], -(NA_KW - 1), NA_KW - 1) + NA_KW - 1

    def one_row(r):
        rs = jnp.clip(r - kh // 2, 0, rows - kh)
        qr = lax.dynamic_index_in_dim(qg, r, axis=1, keepdims=False)
        kb = lax.dynamic_slice_in_dim(kg, rs, kh, axis=1)
        vb = lax.dynamic_slice_in_dim(vg, rs, kh, axis=1)
        s = jnp.einsum('bqhd,bjkhd->bhqjk', qr, kb).astype(jnp.float32)
        dr = rs + jnp.arange(kh) - r + NA_KH - 1
        bias = rpb[:, dr[None, :, None], dc[:, None, :]].astype(jnp.float32)
        s = jnp.where(col_in[:, None, :], s + bias[None], -jnp.inf)
        p = jax.nn.softmax(s.reshape(b, h, GRID_W, kh * GRID_W), axis=-1)
        p = p.reshape(b, h, GRID_W, kh, GRID_W).astype(vb.dtype)
        return jnp.einsum('bhqjk,bjkhd->bqhd', p, vb)

    out = lax.map(one_row, jnp.arange(rows))
    return out.transpose(1, 0, 2, 3, 4).reshape(b, t, h * dh)

def ssd_branch(h, mem_n, w_in, conv_w, conv_b, dt_bias_f, dt_bias_b, a_log_f, a_log_b,
               d_skip, norm_g, w_mem_kv):
    b, t, _ = h.shape
    proj = h @ w_in
    z, xbc, dt_f, dt_b, q_mem = jnp.split(
        proj, [MIX_WIDTH, MIX_WIDTH + SSD_CONV_DIM, MIX_WIDTH + SSD_CONV_DIM + SSD_HEADS,
               MIX_WIDTH + SSD_CONV_DIM + 2 * SSD_HEADS], axis=-1)
    xbc = jax.nn.silu(depthwise_conv_centred(xbc, conv_w, conv_b))
    xs, bm, cm = jnp.split(xbc, [BRANCH_WIDTH, BRANCH_WIDTH + SSD_GROUPS * SSD_STATE], axis=-1)
    xs = xs.reshape(b, t, SSD_HEADS, SSD_HEAD_DIM)
    bm = bm.reshape(b, t, SSD_GROUPS, SSD_STATE)
    cm = cm.reshape(b, t, SSD_GROUPS, SSD_STATE)
    y_fwd = ssd_direction(xs, bm, cm, dt_f, dt_bias_f, a_log_f)
    y_bwd = jnp.flip(ssd_direction(jnp.flip(xs, 1), jnp.flip(bm, 1), jnp.flip(cm, 1),
                                   jnp.flip(dt_b, 1), dt_bias_b, a_log_b), 1)
    y = (y_fwd + y_bwd + d_skip[:, None] * xs).reshape(b, t, BRANCH_WIDTH)
    y = rmsnorm(y * jax.nn.silu(z[..., :BRANCH_WIDTH]), norm_g)
    m = memory_attention(q_mem, mem_n, w_mem_kv) * jax.nn.silu(z[..., BRANCH_WIDTH:])
    return jnp.concatenate([y, m.astype(y.dtype)], axis=-1)

def na_branch(h, mem_n, w_in, rpb, w_mem_kv):
    b, t, _ = h.shape
    proj = h @ w_in
    z, q, k, v, q_mem = jnp.split(
        proj, [MIX_WIDTH, MIX_WIDTH + BRANCH_WIDTH, MIX_WIDTH + 2 * BRANCH_WIDTH,
               MIX_WIDTH + 3 * BRANCH_WIDTH], axis=-1)
    shp = (b, t, NA_HEADS, NA_HEAD_DIM)
    o = neighbourhood_attention(q.reshape(shp), k.reshape(shp), v.reshape(shp), rpb)
    m = memory_attention(q_mem, mem_n, w_mem_kv)
    return jnp.concatenate([o, m.astype(o.dtype)], axis=-1) * jax.nn.silu(z)

def encoder(x, mem, pre_g, post_g, mem_g, w_mem_kv, w_out, ssd_w_in, ssd_conv_w, ssd_conv_b,
            ssd_dt_bias_f, ssd_dt_bias_b, ssd_a_log_f, ssd_a_log_b, ssd_d, ssd_norm_g,
            na_w_in, na_rpb):
    for i in range(DEPTH):
        h = rmsnorm(x, pre_g[i])
        mem_n = rmsnorm(mem, mem_g[i])
        j = i // N_MIXERS
        if i % N_MIXERS == 0:
            mixed = ssd_branch(h, mem_n, ssd_w_in[j], ssd_conv_w[j], ssd_conv_b[j], ssd_dt_bias_f[j],
                               ssd_dt_bias_b[j], ssd_a_log_f[j], ssd_a_log_b[j], ssd_d[j],
                               ssd_norm_g[j], w_mem_kv[i])
        else:
            mixed = na_branch(h, mem_n, na_w_in[j], na_rpb[j], w_mem_kv[i])
        x = x + rmsnorm(mixed @ w_out[i], post_g[i]).astype(x.dtype)
    return x

def setup_inputs(seed: int = 0) -> dict:
    key = jax.random.key(seed)
    ks = jax.random.split(key, 20)
    f32 = jnp.float32

    def nrm(k, shape, scale):
        return jax.random.normal(k, shape, f32) * scale

    def dt_bias(k):
        dt = jnp.exp(jax.random.uniform(k, (N_SSD_LAYERS, SSD_HEADS), f32,
                                        np.log(1e-3), np.log(1e-1)))
        return dt + jnp.log(-jnp.expm1(-dt))

    def a_log(k):
        return jnp.log(jax.random.uniform(k, (N_SSD_LAYERS, SSD_HEADS), f32, 1.0, 16.0))

    return {
        'x_prompt': nrm(ks[0], (BATCH, SEQ, D_MODEL), 1.0),
        'x_sample': nrm(ks[1], (DEC_BATCH, DEC_SEQ, D_MODEL), 1.0),
        'mem_prompt': nrm(ks[2], (BATCH, MEM_TOKENS, D_MODEL), 1.0),
        'mem_sample': nrm(ks[3], (DEC_BATCH, MEM_TOKENS, D_MODEL), 1.0),
        'pre_g': 1.0 + nrm(ks[4], (DEPTH, D_MODEL), 0.02),
        'post_g': 1.0 + nrm(ks[5], (DEPTH, D_MODEL), 0.02),
        'mem_g': 1.0 + nrm(ks[6], (DEPTH, D_MODEL), 0.02),
        'w_mem_kv': nrm(ks[7], (DEPTH, D_MODEL, 2 * MEM_WIDTH), D_MODEL ** -0.5),
        'w_out': nrm(ks[8], (DEPTH, MIX_WIDTH, D_MODEL), MIX_WIDTH ** -0.5),
        'ssd_w_in': nrm(ks[9], (N_SSD_LAYERS, D_MODEL, SSD_IN), D_MODEL ** -0.5),
        'ssd_conv_w': nrm(ks[10], (N_SSD_LAYERS, SSD_CONV, SSD_CONV_DIM), SSD_CONV ** -0.5),
        'ssd_conv_b': nrm(ks[11], (N_SSD_LAYERS, SSD_CONV_DIM), 0.02),
        'ssd_dt_bias_f': dt_bias(ks[12]),
        'ssd_dt_bias_b': dt_bias(ks[13]),
        'ssd_a_log_f': a_log(ks[14]),
        'ssd_a_log_b': a_log(ks[15]),
        'ssd_d': 1.0 + nrm(ks[16], (N_SSD_LAYERS, SSD_HEADS), 0.02),
        'ssd_norm_g': 1.0 + nrm(ks[17], (N_SSD_LAYERS, BRANCH_WIDTH), 0.02),
        'na_w_in': nrm(ks[18], (N_NA_LAYERS, D_MODEL, NA_IN), D_MODEL ** -0.5),
        'na_rpb': nrm(ks[19], (N_NA_LAYERS, NA_HEADS, 2 * NA_KH - 1, 2 * NA_KW - 1), 0.1),
    }

def reference(x_prompt, x_sample, mem_prompt, mem_sample, pre_g, post_g, mem_g, w_mem_kv, w_out,
              ssd_w_in, ssd_conv_w, ssd_conv_b, ssd_dt_bias_f, ssd_dt_bias_b, ssd_a_log_f,
              ssd_a_log_b, ssd_d, ssd_norm_g, na_w_in, na_rpb):
    y_prompt = encoder(x_prompt, mem_prompt, pre_g, post_g, mem_g, w_mem_kv, w_out, ssd_w_in,
                       ssd_conv_w, ssd_conv_b, ssd_dt_bias_f, ssd_dt_bias_b, ssd_a_log_f,
                       ssd_a_log_b, ssd_d, ssd_norm_g, na_w_in, na_rpb)
    y_sample = encoder(x_sample, mem_sample, pre_g, post_g, mem_g, w_mem_kv, w_out, ssd_w_in,
                       ssd_conv_w, ssd_conv_b, ssd_dt_bias_f, ssd_dt_bias_b, ssd_a_log_f,
                       ssd_a_log_b, ssd_d, ssd_norm_g, na_w_in, na_rpb)
    return (y_prompt, y_sample)


_drawn_inputs = setup_inputs


def setup_inputs(seed=0):
    import zlib

    import numpy as np

    out = dict(_drawn_inputs(seed))
    spreads = {}
    factors = {'mem_g': 8.0, 'ssd_d': 14.027, 'ssd_norm_g': 8.413, 'na_rpb': 22.668}
    for name, (base, spread) in spreads.items():
        noise = np.random.default_rng([zlib.crc32(name.encode()), seed]).standard_normal(out[name].shape)
        drawn = base * np.exp(spread * noise) if base else spread * noise
        out[name] = jnp.asarray(drawn.astype(out[name].dtype))
    for name, factor in factors.items():
        out[name] = (out[name] * factor).astype(out[name].dtype)
    return out
```

```python
from contextlib import ExitStack

import concourse.bass as bass
from concourse import mybir

P = 128
D = 1024
KC = D // P
NP_, NS = 256, 512
T = NP_ + NS
NT = T // P
MIX = 3072
INNER = 2048
CONV = 3072
HEADS = 32
PAIRS = HEADS // 2
GRIDW = 64
EPS = 1e-6
F32, F32R = mybir.dt.float32, mybir.dt.float32r
ALU, ACT = mybir.AluOpType, mybir.ActivationFunctionType
AXX = mybir.AxisListType.X
NEG = -1e30
SPAN = [(0, NP_), (NP_, T)]
S_XBC, S_DT, S_Q = MIX, MIX + CONV, MIX + CONV + 2 * HEADS
N_Q, N_K, N_V, N_QM = MIX, MIX + INNER, MIX + 2 * INNER, MIX + 3 * INNER


DVE_PER = 167


class Count:

    def __init__(self, start=0):
        self.base, self.k, self.start, self.per = 0, start, start, None

    def enter(self, i, per):
        self.at, self.per, self.base = self.k, per, i * per

    def leave(self, trips):
        assert self.k - self.at == self.per, (self.k - self.at, self.per)
        self.k, self.base = self.at + self.per * trips, 0

    def next(self):
        self.k += 1

    @property
    def value(self):
        return self.base + self.k


class Chain:

    def __init__(self, eng, sem, start=0):
        self.eng, self.sem, self.n = eng, sem, Count(start)

    def add(self, ins):
        ins.then_inc(self.sem, 1)
        self.n.next()
        return self.n.value

    def wait(self, value=None):
        self.eng.wait_ge(self.sem, self.n.value if value is None else value)

    def link(self, ins):
        self.add(ins)
        self.wait()


def encoder_kernel(nc, x_prompt, x_sample, mem_prompt, mem_sample, pre_g, post_g, mem_g, w_mem_kv, w_out,
                   ssd_w_in, ssd_conv_w, ssd_conv_b, ssd_dt_bias_f, ssd_dt_bias_b, ssd_a_log_f,
                   ssd_a_log_b, ssd_d, ssd_norm_g, na_w_in, na_rpb, y_prompt, y_sample):
    ctx = ExitStack()
    with ctx:
        ctx.enter_context(nc.allow_non_contiguous_dma(reason="small constants"))

        def sb(name, shape, dt=F32):
            return ctx.enter_context(nc.sbuf_tensor(name, shape, dt))

        def sem(name):
            return ctx.enter_context(nc.semaphore(name))

        Hh, Hl = sb("Hh", [P, KC, T], F32R), sb("Hl", [P, KC, T], F32R)
        Wraw = sb("Wraw", [P, 2, 1024])
        Wh, Wl = sb("Wh", [P, 2, 1024], F32R), sb("Wl", [P, 2, 1024], F32R)
        Mh, Ml = sb("Mh", [P, 2, T], F32R), sb("Ml", [P, 2, T], F32R)
        acc = sb("acc", [P, NT, D])
        ident, mask_u, mask_l, ones = (sb(n, [P, P]) for n in ("ident", "mask_u", "mask_l", "ones"))
        eps = sb("eps", [P, 1])
        rssd = sb("rssd", [P, NT])
        NR = 24800
        R = sb("R", [P, NR])
        bank = [ctx.enter_context(nc.psum_tensor(f"bank{i}", [P, 512], F32)) for i in range(8)]
        DB, A = bank[0:2], bank[2:8]

        class Region:
            def __init__(self):
                self.at = 0

            def __call__(self, *dims):
                n = 1
                for d in dims:
                    n *= d
                v = R[:, self.at:self.at + n]
                self.at += n
                assert self.at <= NR, self.at
                if len(dims) == 1:
                    return v
                names = "abcd"[:len(dims)]
                kw = {names[i]: dims[i] for i in range(1, len(dims))}
                return v.rearrange(f"p ({' '.join(names)}) -> p {' '.join(names)}", **kw)

        def dram(name, shape):
            return nc.dram_tensor(name, shape, F32, kind="Internal").ap()

        x1_dram = dram("x1_dram", [T, D])
        macc_dram = dram("macc_dram", [T, D])
        acs_dram = dram("acs_dram", [2 * HEADS, T])
        rp_dram = dram("rp_dram", [HEADS, 15, 80])
        gs_dram = dram("gs_dram", [HEADS, 16, 15, 32])
        gp_dram = dram("gp_dram", [HEADS, 32, 7, 48])

        raw_landed = [sem("raw_landed0"), sem("raw_landed1")]
        w_ready, unit_done = sem("w_ready"), sem("unit_done")
        half_done, dense_free = sem("half_done"), sem("dense_free")
        out_done, out_added = sem("out_done"), sem("out_added")
        mix_ready = sem("mix_ready")
        passed = sem("passed")
        dve_c, act_c, pool_c = sem("dve_c"), sem("act_c"), sem("pool_c")

        U = {k: Count() for k in ("sp", "pool", "pe", "act", "dve")}
        HF, HD = ({k: Count() for k in ("pe", "act", "dve")} for _ in range(2))
        OF, OD = ({k: Count() for k in ("pe", "dve", "sp")} for _ in range(2))
        MX = {k: Count() for k in ("pe", "dve")}
        CH = {"dve": Count(), "act": Count(), "pool": Count()}

        def chain(eng, name):
            c = Chain(eng, {"dve": dve_c, "act": act_c, "pool": pool_c}[name])
            c.n = CH[name]
            return c

        def load_unit(sp, src, dims):
            s = U["sp"].k % 2
            dst = Wraw[:, s, :].rearrange("p (k c) -> p k c", k=dims)
            sp.wait_ge(w_ready, U["sp"].value + 1)
            settle(sp)
            sp.dma_start(dst, src).then_inc(raw_landed[s], 16)
            U["sp"].next()

        def load_f(sp, w, col):
            load_unit(sp, w.rearrange("(k p) c -> p k c", p=P)[:, :, col], KC)

        def load_out(sp, layer, rows):
            w = w_out[layer, rows, :].rearrange("(k p) c -> p k c", p=P)
            for h in range(2):
                load_unit(sp, w[:, :, h * 512:(h + 1) * 512], 2)

        def split_unit(pool):
            u, c = U["pool"], CH["pool"]
            s = u.k % 2
            pool.wait_ge(raw_landed[s], u.base * 8 + 16 * (u.k // 2 + 1))
            pool.wait_ge(unit_done, u.value + 1)
            settle(pool)
            pool.tensor_scalar(Wh[:, s, :], Wraw[:, s, :], 1.0, 1.0, ALU.mult, ALU.mult).then_inc(pool_c, 1)
            c.next()
            pool.wait_ge(pool_c, c.value)
            pool.tensor_tensor(Wl[:, s, :], Wraw[:, s, :], Wh[:, s, :].bitcast(F32), ALU.subtract)\
                .then_inc(w_ready, 1)
            u.next()

        def settle(eng):
            eng.sem_inc(passed, 1)

        def pe_dense(pe, spans=SPAN, units=1):
            u, h, hd = U["pe"], HF["pe"], HD["pe"]
            s = u.k % 2
            pe.wait_ge(w_ready, u.value + 3)
            wh = Wh[:, s, :].rearrange("p (k c) -> p k c", k=KC)
            wl = Wl[:, s, :].rearrange("p (k c) -> p k c", k=KC)
            for t0, t1 in spans:
                pe.wait_ge(dense_free, h.value + 1)
                for k in range(KC):
                    for i, (w, x) in enumerate(((wh, Hh), (wh, Hl), (wl, Hh))):
                        mm = pe.matmul(DB[h.k % 2][:, 0:t1 - t0], w[:, k, :], x[:, k, t0:t1],
                                       start=(k == 0 and i == 0), stop=(k == KC - 1 and i == 2))
                h.next()
                if t1 == spans[-1][1]:
                    mm.then_inc(unit_done, units)
                else:
                    mm.then_inc(half_done, 1)
                    hd.next()
            for _ in range(units):
                u.next()

        def act_take(act, fns, units=1):
            u, h, hd = U["act"], HF["act"], HD["act"]
            for n, fn in enumerate(fns):
                if n < len(fns) - 1:
                    act.wait_ge(half_done, hd.value + 1)
                    hd.next()
                else:
                    for _ in range(units):
                        u.next()
                    act.wait_ge(unit_done, u.value + 2)
                fn(DB[h.k % 2]).then_inc(dense_free, 1)
                h.next()

        def take_spans(act, dst, func=ACT.Copy, scale=1.0):
            act_take(act, [lambda b: act.activation(dst[:, 0:NP_], b[:, 0:NP_], func, scale=scale),
                           lambda b: act.activation(dst[:, NP_:T], b[:, 0:NS], func, scale=scale)])

        def pe_out(pe):
            u, o, od, m = U["pe"], OF["pe"], OD["pe"], MX["pe"]
            m.next()
            pe.wait_ge(mix_ready, m.value)
            for half in range(2):
                s = u.k % 2
                pe.wait_ge(w_ready, u.value + 3)
                wh = Wh[:, s, :].rearrange("p (k c) -> p k c", k=2)
                wl = Wl[:, s, :].rearrange("p (k c) -> p k c", k=2)
                for i in range(NT):
                    pe.wait_ge(out_added, o.value + 1)
                    for k in range(2):
                        for j, (x, w) in enumerate(((Mh, wh), (Ml, wh), (Mh, wl))):
                            mm = pe.matmul(A[4 + o.k % 2][:, :], x[:, k, i * P:(i + 1) * P], w[:, k, :],
                                           start=(k == 0 and j == 0), stop=(k == 1 and j == 2))
                    o.next()
                    if i < NT - 1:
                        mm.then_inc(out_done, 1)
                        od.next()
                    else:
                        mm.then_inc(unit_done, 1)
                u.next()

        def dve_out(dve):
            u, o, od = U["dve"], OF["dve"], OD["dve"]
            for half in range(2):
                u.next()
                for i in range(NT):
                    dst = acc[:, i, half * 512:(half + 1) * 512]
                    if i < NT - 1:
                        od.next()
                        dve.wait_ge(out_done, od.value)
                    else:
                        dve.wait_ge(unit_done, u.value + 2)
                    dve.tensor_tensor(dst, A[4 + o.k % 2][:, :], dst, ALU.add).then_inc(out_added, 1)
                    o.next()

        def loop(eng, trips, counts):
            class L:
                def __enter__(s):
                    s.l = eng.Fori(0, trips)
                    i = s.l.__enter__()
                    for c, per in counts:
                        c.enter(i, per)
                    return i

                def __exit__(s, *a):
                    r = s.l.__exit__(*a)
                    if a[0] is None:
                        for c, _ in counts:
                            c.leave(trips)
                    return r
            return L()

        def setup():
            with nc.Block() as block:
                @block.gpsimd
                def _(pool):
                    c = chain(pool, "pool")
                    pool.sem_inc(w_ready, 2)
                    c.add(pool.memset(ident[:, :], 0.0))
                    c.add(pool.memset(mask_u[:, :], 1.0))
                    c.add(pool.memset(mask_l[:, :], 1.0))
                    c.add(pool.memset(ones[:, :], 1.0))
                    c.link(pool.memset(eps[:, :], EPS))
                    c.add(pool.affine_select(out=ident[:, :], in_=ident[:, :], compare_op=ALU.not_equal, fill=1.0,
                                             base=0, pattern=[[-1, P]], channel_multiplier=1))
                    c.add(pool.affine_select(out=mask_u[:, :], in_=mask_u[:, :], compare_op=ALU.is_ge, fill=0.0,
                                             base=0, pattern=[[1, P]], channel_multiplier=-1))
                    c.link(pool.affine_select(out=mask_l[:, :], in_=mask_l[:, :], compare_op=ALU.is_ge, fill=0.0,
                                              base=0, pattern=[[-1, P]], channel_multiplier=1))

                @block.tensor
                def _(pe):
                    pe.sem_inc(unit_done, 2)

                @block.scalar
                def _(act):
                    act.sem_inc(dense_free, 2)

                @block.vector
                def _(dve):
                    dve.sem_inc(out_added, 2)

        class Norm:

            def __init__(self, name, tiles, gain, where, xn, small, h_free):
                self.tiles, self.gain, self.where, self.xn, self.h_free = tiles, gain, where, xn, h_free
                self.ss, self.sd, self.r = small
                self.sums, self.roots, self.normed, self.turned, self.hi, self.lo = (
                    sem(f"{name}_{x}") for x in ("sums", "roots", "normed", "turned", "hi", "lo"))

            def act(self, act, ready=None, junk=None):
                n = len(self.tiles)
                for i, x in enumerate(self.tiles):
                    if ready is not None:
                        ready(act, i)
                    if i:
                        act.wait_ge(self.sums, i)
                    act.activation(junk, x, ACT.Square, accum_out=self.ss[:, i:i + 1]).then_inc(self.sums, 1)
                act.wait_ge(self.sums, n)
                act.activation(self.sd[:, 0:n], self.ss[:, 0:n], ACT.Sqrt, scale=1.0 / D, bias=eps[:, 0:1])\
                    .then_inc(self.roots, 1)
                self.h_free(act)
                for i in range(n):
                    for half in range(2):
                        act.wait_ge(self.turned, 2 * i + half + 1)
                        k = slice(4 * half, 4 * half + 4)
                        act.activation(self.where(Hh, k, i), self.src(i, half), ACT.Copy).then_inc(self.hi, 1)

            def src(self, i, half):
                b = A[(2 * i + half) % 4][:, :]
                if self.where.rows is None or self.where.rows(i) is None:
                    return b.rearrange("p (k t) -> p k t", k=4)
                return b.rearrange("p (k r c) -> p k r c", k=4, r=2)

            def dve(self, dve, c):
                n = len(self.tiles)
                dve.wait_ge(self.roots, 1)
                c.link(dve.reciprocal(self.r[:, 0:n], self.sd[:, 0:n]))

                def lo(i):
                    for half in range(2):
                        k = slice(4 * half, 4 * half + 4)
                        dve.wait_ge(self.hi, 2 * i + half + 1)
                        dve.tensor_tensor(self.where(Hl, k, i), self.src(i, half),
                                          self.where(Hh, k, i).bitcast(F32), ALU.subtract).then_inc(self.lo, 1)

                for i in range(n):
                    if i >= 2:
                        dve.wait_ge(self.turned, 2 * (i - 1))
                    dve.scalar_tensor_tensor(self.xn[i % 2], self.tiles[i], self.r[:, i:i + 1], self.gain,
                                             ALU.mult, ALU.mult).then_inc(self.normed, 1)
                    if i >= 1:
                        lo(i - 1)
                lo(n - 1)

            def pe(self, pe):
                for i in range(len(self.tiles)):
                    pe.wait_ge(self.normed, i + 1)
                    for half in range(2):
                        if 2 * i + half >= 4:
                            pe.wait_ge(self.lo, 2 * i + half - 3)
                        for k in range(4):
                            kk = 4 * half + k
                            mm = pe.transpose(A[(2 * i + half) % 4][:, k * P:(k + 1) * P],
                                              self.xn[i % 2][:, kk * P:(kk + 1) * P], ident[:, :])
                        mm.then_inc(self.turned, 1)
                pe.wait_ge(self.lo, 2 * len(self.tiles))

        class InOrder:
            rows = None

            def __call__(self, H, k, i):
                return H[:, k, i * P:(i + 1) * P]

        class ByColumn:

            def rows(self, i):
                return 4 if i < 2 else 8

            def __call__(self, H, k, i):
                t0, t1 = SPAN[0] if i < 2 else SPAN[1]
                r, i = (4, i) if i < 2 else (8, i - 2)
                return H[:, k, t0:t1].rearrange("p k (c r) -> p k r c", r=r)[:, :, 2 * i:2 * i + 2, :]

        def memory_phase(L):
            w_in = (ssd_w_in if L == 0 else na_w_in)[0]
            q_col, z_col = (S_Q if L == 0 else N_QM), INNER
            wkv = w_mem_kv[L]
            r = Region()
            kT, vtok = r(8, 512), r(4, D)
            gm, gp = r(D), r(D)
            xn = [r(D), r(D)]
            junk = xn[0]
            small = [r(10) for _ in range(3)]
            mem = r(4, D)
            vF = [r(512), r(512)]
            qm, zm = mem[:, 0:2, 0:T], mem[:, 2:4, 0:T]
            prob, pT, vh = r(NT, 256), r(2, T), r(4, 256)
            gated = r(2, T)
            nmax, psum_, pinv = r(NT), r(NT), r(NT)
            n = f"m{L}_"
            in_landed = [sem(f"{n}landed{i}") for i in range(4)]
            gain_landed = sem(n + "gain_landed")
            v_turned, v_ready, vh_ready, scored, max_ready, prob_ready, prob_normed = (
                sem(n + x) for x in ("v_turned", "v_ready", "vh_ready", "scored", "max_ready", "prob_ready",
                                     "prob_normed"))
            p_turned, pT_ready, mixed, gate_ready, hi_ready = (
                sem(n + x) for x in ("p_turned", "pT_ready", "mixed", "gate_ready", "hi_ready"))
            stored = sem(n + "stored")
            where = InOrder() if L == 0 else ByColumn()

            def timed(x, q, out):
                if L == 0:
                    return x
                pat = "(r c) -> {} c r" if out else "(c r) -> {} c r"
                lead = "p f" if len(x.shape) == 3 else "p"
                return x.rearrange(f"{lead} {pat.format(lead)}", r=(4, 8)[q])

            kv_units = U["pe"].k + 16

            def h_used_by_kv(eng):
                eng.wait_ge(unit_done, kv_units + 2)

            mem_norm = Norm(n + "nm", [mem[:, i, :] for i in range(4)], gm, InOrder(), xn, small,
                            lambda eng: None)
            x_norm = Norm(n + "nx", [acc[:, i, :] for i in range(NT)], gp, where, xn, small, h_used_by_kv)
            x_norm.ss, x_norm.sd, x_norm.r = (s[:, 4:10] for s in small)
            group = [0, 0, 1, 1, 1, 1]

            with nc.Block() as block:
                @block.sync
                def _(sp):
                    for i in range(2):
                        src = (mem_prompt if i == 0 else mem_sample)[0].rearrange("(i p) c -> p i c", p=P)
                        sp.dma_start(mem[:, 2 * i:2 * i + 2, :], src).then_inc(in_landed[i], 16)
                    sp.dma_start(gm, mem_g[L:L + 1, :].broadcast_to([P, D])).then_inc(gain_landed, 16)
                    if L == 0:
                        sp.dma_start(acc[:, 0:2, :], x_prompt[0].rearrange("(i p) c -> p i c", p=P))\
                            .then_inc(in_landed[2], 16)
                        sp.dma_start(acc[:, 2:6, :], x_sample[0].rearrange("(i p) c -> p i c", p=P))\
                            .then_inc(in_landed[3], 16)
                    sp.dma_start(gp, pre_g[L:L + 1, :].broadcast_to([P, D])).then_inc(gain_landed, 16)
                    with loop(sp, 8, [(U["sp"], 2)]) as i:
                        for s in range(2):
                            load_f(sp, wkv, bass.ds(i * 256 + s * P, P))
                    with loop(sp, 4, [(U["sp"], 6)]) as i:
                        for base in (q_col, z_col):
                            for s in range(2):
                                load_f(sp, w_in, bass.ds(i * 256 + (base + s * P), P))
                        load_out(sp, L, bass.ds(i * 256 + INNER, 256))
                    OF["sp"].k += 4 * 2 * NT
                    if L == 0:
                        sp.wait_ge(out_added, OF["sp"].value + 2)
                        sp.dma_start(macc_dram.rearrange("(i p) c -> p i c", p=P), acc[:, :, :])\
                            .then_inc(stored, 16)
                        sp.wait_ge(stored, 16)

                @block.gpsimd
                def _(pool):
                    chain(pool, "pool")
                    with loop(pool, 20, [(U["pool"], 2), (CH["pool"], 2)]):
                        for s in range(2):
                            split_unit(pool)

                @block.scalar
                def _(act):
                    mem_norm.act(act, lambda e, i: e.wait_ge(in_landed[i // 2], 16) if i % 2 == 0 else None, junk)
                    with loop(act, 4, [(U["act"], 2), (HF["act"], 2)]) as i:
                        for s in range(2):
                            act_take(act, [lambda b: act.activation(
                                kT[:, bass.ds(i * 2 + s, 1), :].rearrange("p a t -> p (a t)"), b[:, :], ACT.Copy)])
                    with loop(act, 4, [(U["act"], 2), (HF["act"], 2)]) as i:
                        for s in range(2):
                            act.wait_ge(v_turned, i * 2 + (s + 1))
                            act_take(act, [lambda b: act.activation(vF[s], b[:, :], ACT.Copy)])
                    x_norm.act(act, (lambda e, i: e.wait_ge(in_landed[2 + i // 2 if i < 2 else 3], 16)
                                     if i in (0, 2) else None) if L == 0 else None, junk)
                    with loop(act, 4, [(U["act"], 6), (HF["act"], 8), (HD["act"], 4)]) as i:
                        for s in range(2):
                            take_spans(act, qm[:, s, :], scale=1.0 / 16)
                        for s in range(2):
                            take_spans(act, zm[:, s, :], ACT.Silu)
                        for t in range(NT):
                            if t % 2 == 0:
                                act.wait_ge(max_ready, i * 3 + (t // 2 + 1))
                            act.activation(prob[:, t, :], A[t // 2][:, (t % 2) * 256:(t % 2 + 1) * 256], ACT.Exp,
                                           bias=nmax[:, t:t + 1], accum_out=psum_[:, t:t + 1])\
                                .then_inc(prob_ready, 1)
                        act.wait_ge(p_turned, i * 3 + 1)
                        act.activation(pT[:, :, 0:NP_], A[3][:, :].rearrange("p (m t) -> p m t", m=2), ACT.Copy)\
                            .then_inc(pT_ready, 1)
                        for m in range(2):
                            act.wait_ge(p_turned, i * 3 + (2 + m))
                            act.activation(pT[:, m, NP_:T], A[4 + m][:, :], ACT.Copy).then_inc(pT_ready, 1)
                        act.wait_ge(gate_ready, i * 3 + 3)
                        act.activation(Mh[:, :, :], gated, ACT.Copy).then_inc(hi_ready, 1)
                        for _ in range(2):
                            U["act"].next()

                @block.vector
                def _(dve):
                    c = chain(dve, "dve")
                    dve.sem_inc(v_ready, 2)
                    dve.wait_ge(gain_landed, 32)
                    mem_norm.dve(dve, c)

                    with loop(dve, 4, [(U["dve"], 0)]) as i:
                        for s in range(2):
                            dve.wait_ge(v_turned, i * 2 + (s + 3))
                            dve.tensor_copy(vtok[:, :, bass.ds(i * 256 + s * P, P)],
                                            A[s][:, :].rearrange("p (t f) -> p t f", t=4)).then_inc(v_ready, 1)
                    for _ in range(16):
                        U["dve"].next()
                        HF["dve"].next()
                    x_norm.dve(dve, c)
                    dve.wait_ge(x_norm.normed, NT)
                    c.link(dve.memset(acc[:, :, :], 0.0))
                    with loop(dve, 4, [(U["dve"], 6), (OF["dve"], 12), (OD["dve"], 10), (CH["dve"], 1), (HF["dve"], 8)]) as i:
                        dve.tensor_copy(vh, vtok[:, :, bass.ds(i * 256, 256)]).then_inc(vh_ready, 1)
                        for b in range(3):
                            dve.wait_ge(scored, i * 3 + (b + 1))
                            dve.tensor_reduce(nmax[:, 2 * b:2 * b + 2],
                                              A[b][:, :].rearrange("p (t m) -> p t m", t=2),
                                              AXX, ALU.max, negate=True).then_inc(max_ready, 1)
                        dve.wait_ge(prob_ready, i * NT + NT)
                        c.link(dve.reciprocal(pinv, psum_))
                        for t in range(NT):
                            dve.tensor_scalar(prob[:, t, :], prob[:, t, :], pinv[:, t:t + 1], None, ALU.mult)\
                                .then_inc(prob_normed, 1)
                        for _ in range(8):
                            HF["dve"].next()
                        dve.wait_ge(dense_free, HF["dve"].value + 2)
                        dve.wait_ge(mixed, i * 3 + 1)
                        dve.tensor_tensor(timed(gated[:, :, 0:NP_], 0, True),
                                          timed(A[0][:, :].rearrange("p (f t) -> p f t", f=2), 0, False),
                                          timed(zm[:, :, 0:NP_], 0, False), ALU.mult).then_inc(gate_ready, 1)
                        for f in range(2):
                            dve.wait_ge(mixed, i * 3 + (2 + f))
                            dve.tensor_tensor(timed(gated[:, f, NP_:T], 1, True), timed(A[1 + f][:, :], 1, False),
                                              timed(zm[:, f, NP_:T], 1, False), ALU.mult).then_inc(gate_ready, 1)
                        dve.wait_ge(hi_ready, i + 1)
                        dve.tensor_tensor(Ml[:, :, :], gated, Mh[:, :, :].bitcast(F32), ALU.subtract)\
                            .then_inc(mix_ready, 1)
                        for _ in range(4):
                            U["dve"].next()
                        dve_out(dve)

                @block.tensor
                def _(pe):
                    mem_norm.pe(pe)
                    pe.sem_inc(v_turned, 2)
                    kv = [(0, 512)]
                    with loop(pe, 4, [(U["pe"], 2), (HF["pe"], 2)]):
                        for s in range(2):
                            pe_dense(pe, kv)
                    with loop(pe, 4, [(U["pe"], 2), (HF["pe"], 2)]) as i:
                        for s in range(2):
                            pe_dense(pe, kv)
                            pe.wait_ge(dense_free, HF["pe"].value + 2)
                            pe.wait_ge(v_ready, i * 2 + (s + 1))
                            for t in range(4):
                                mm = pe.transpose(A[s][:, t * P:(t + 1) * P], vF[s][:, t * P:(t + 1) * P],
                                                  ident[:, :])
                            mm.then_inc(v_turned, 1)
                    pe.wait_ge(v_ready, 10)
                    x_norm.pe(pe)
                    with loop(pe, 4, [(U["pe"], 6), (HF["pe"], 8), (HD["pe"], 4), (OF["pe"], 12), (OD["pe"], 10),
                                      (MX["pe"], 1)]) as i:
                        pe_dense(pe)
                        pe_dense(pe)
                        pe.wait_ge(dense_free, HF["pe"].value + 2)
                        for t in range(NT):
                            for k in range(2):
                                mm = pe.matmul(A[t // 2][:, (t % 2) * 256:(t % 2 + 1) * 256],
                                               qm[:, k, t * P:(t + 1) * P],
                                               kT[:, bass.ds(i * 2 + k, 1), group[t] * 256:(group[t] + 1) * 256]
                                               .rearrange("p a t -> p (a t)"), start=(k == 0), stop=(k == 1))
                            if t % 2:
                                mm.then_inc(scored, 1)
                        pe_dense(pe)
                        pe_dense(pe)
                        pe.wait_ge(out_added, OF["pe"].value + 2)
                        for t in range(NT):
                            pe.wait_ge(prob_normed, i * NT + (t + 1))
                            for m in range(2):
                                out = A[3][:, m * 256 + t * P:m * 256 + (t + 1) * P] if t < 2 else \
                                    A[4 + m][:, (t - 2) * P:(t - 1) * P]
                                mm = pe.transpose(out, prob[:, t, m * P:(m + 1) * P], ident[:, :])
                                if t == 1 and m == 1 or t == NT - 1:
                                    mm.then_inc(p_turned, 1)
                        pe.wait_ge(vh_ready, i + 1)
                        pe.wait_ge(pT_ready, i * 3 + 3)
                        for f in range(2):
                            for m in range(2):
                                mm = pe.matmul(A[0][:, f * 256:(f + 1) * 256], vh[:, m, f * P:(f + 1) * P],
                                               pT[:, m, 0:NP_], start=(m == 0), stop=(m == 1))
                        mm.then_inc(mixed, 1)
                        for f in range(2):
                            for m in range(2):
                                mm = pe.matmul(A[1 + f][:, :], vh[:, 2 + m, f * P:(f + 1) * P],
                                               pT[:, m, NP_:T], start=(m == 0), stop=(m == 1))
                            mm.then_inc(mixed, 1)
                        pe_out(pe)

        def ssd_phase():
            w_in = ssd_w_in[0]
            r = Region()
            raw = r(2, T + 6)
            conv = r(T + 2)
            xs = r(2, T)
            xtok = r(2, NT, P)
            xw = r(2, NT, P)
            bT, cT = r(T), r(T)
            btok = r(NT, P)
            cb_u, cb_l = r(NT, P), r(NT, P)
            ab = r(2, 2, T)
            eab = r(2, T)
            seg, tmp2 = r(4, 2, P), r(4, 2, P)
            dec = r(NT, 2, P)
            z, y = r(T), r(T)
            prev = r(2, 4, P)
            dt_tok, acs_tok, w_tok, tot_tok = (r(NT, 64) for _ in range(4))
            sqsum = r(T)
            cw = r(160)
            dcol = r(PAIRS)
            dtb, alog, ea = r(1), r(1), r(1)
            sd = r(NT)
            tmp = conv[:, 0:T]
            dtf, dx, du, dw, dl, acsf = xs[:, 0, :], xs[:, 1, :], bT, cT, z, y
            af = xtok[:, 0, :, :].rearrange("p c l -> p (c l)")
            a_tok = xw[:, 0, 0:3, :].rearrange("p c l -> p (c l)").rearrange("p (c h) -> p c h", h=64)
            stage = cb_u[:, 0:2, :]

            cst = [sem(f"g_const{i}") for i in range(3)]
            (cw_turned, dt_steps, dt_dve, dt_pe, acs_stored, ab_landed, conv_done, silu_done, bc_done, bc_taken,
             x_turned, x_taken, xw_ready, states_done, carried, off_done, diag_done, dec_ready, seg_ready,
             exp_done, eab_done, gated, hi_ready, summed, rooted) = (
                sem("g_" + x) for x in (
                    "cw_turned", "dt_steps", "dt_dve", "dt_pe", "acs_stored", "ab_landed", "conv_done", "silu_done",
                    "bc_done", "bc_taken", "x_turned", "x_taken", "xw_ready", "states_done", "carried",
                    "off_done", "diag_done", "dec_ready", "seg_ready", "exp_done", "eab_done", "gated",
                    "hi_ready", "summed", "rooted"))
            zeroed, padded, expanded = sem("g_zeroed"), sem("g_padded"), sem("g_expanded")
            F_DST, B_DST = (1, 3, 4, 5), (0, 2, 3, 4)
            F_SRC, B_SRC = (0, 2, 3, 4), (1, 3, 4, 5)
            PARTS = [(0, 2), (2, 6)]
            H64 = [slice(0, 64), slice(64, 128)]

            with nc.Block() as block:
                @block.sync
                def _(sp):
                    sp.dma_start(stage[0:120, 0, :], ssd_conv_w[0].rearrange("k (m p) -> (k m) p", p=P))\
                        .then_inc(cst[0], 16)
                    sp.dma_start(stage[0:24, 1, :], ssd_conv_b[0].rearrange("(m p) -> m p", p=P)).then_inc(cst[0], 16)
                    sp.dma_start(stage[24:40, 1, :], ssd_norm_g[0].rearrange("(m p) -> m p", p=P)).then_inc(cst[0], 16)
                    for d, (b, al) in enumerate(((ssd_dt_bias_f, ssd_a_log_f), (ssd_dt_bias_b, ssd_a_log_b))):
                        rows = slice(32 * d, 32 * d + 32)
                        sp.dma_start(dtb[rows, :], b[0].rearrange("(h o) -> h o", o=1)).then_inc(cst[1], 16)
                        sp.dma_start(alog[rows, :], al[0].rearrange("(h o) -> h o", o=1)).then_inc(cst[1], 16)
                    for h in range(2):
                        sp.dma_start(dcol[H64[h], :], ssd_d[0].rearrange("(n h) -> h n", h=2)[h:h + 1, :]
                                     .broadcast_to([64, PAIRS])).then_inc(cst[2], 16)
                    for _ in range(2):
                        load_f(sp, w_in, slice(S_DT, S_DT + P))
                    sp.wait_ge(zeroed, 1)
                    sp.dma_start(rp_dram.rearrange("h r c -> (h r c)").rearrange("(p x) -> p x", p=P),
                                 raw.rearrange("p a x -> p (a x)")[:, 0:300]).then_inc(padded, 16)
                    sp.wait_ge(padded, 16)
                    sp.dma_start(rp_dram[:, :, 24:55], na_rpb[0]).then_inc(padded, 16)
                    sp.wait_ge(padded, 32)
                    for rr in range(15):
                        src = bass.AP(rp_dram.tensor, (14 - rr) * 80 + 31, [[1200, HEADS], [-1, 16], [1, 32]])
                        sp.dma_start(gs_dram[:, :, rr, :], src).then_inc(expanded, 16)
                    for rr in range(7):
                        src = bass.AP(rp_dram.tensor, (10 - rr) * 80 + 31, [[1200, HEADS], [-1, 32], [1, 48]])
                        sp.dma_start(gp_dram[:, :, rr, :], src).then_inc(expanded, 16)
                    sp.wait_ge(dt_steps, 8)
                    sp.dma_start(acs_dram, acsf[0:64, :]).then_inc(acs_stored, 16)
                    sp.wait_ge(acs_stored, 16)

                    def load_ab(n):
                        sp.wait_ge(seg_ready, n * 2 + 1)
                        settle(sp)
                        sp.wait_ge(eab_done, n + 1)
                        settle(sp)
                        sp.dma_start(ab.rearrange("p d h t -> p d (h t)"),
                                     acs_dram.rearrange("(d h) t -> d (h t)", d=2)[:, bass.ds(n * (2 * T), 2 * T)]
                                     .unsqueeze(0).broadcast_to([P, 2, 2 * T])).then_inc(ab_landed, 16)

                    with loop(sp, 4, [(U["sp"], 14)]) as g:
                        load_f(sp, w_in, bass.ds(g * P + (S_XBC + INNER), P))
                        load_f(sp, w_in, bass.ds(g * P + (S_XBC + INNER + 512), P))
                        for p in range(2):
                            for a in range(2):
                                load_f(sp, w_in, bass.ds(g * 512 + (S_XBC + (2 * p + a) * P), P))
                            for a in range(2):
                                load_ab(g * 4 + (2 * p + a))
                                load_f(sp, w_in, bass.ds(g * 512 + (2 * p + a) * P, P))
                            load_out(sp, 0, bass.ds(g * 512 + p * 256, 256))
                    sp.wait_ge(expanded, 22 * 16)

                @block.gpsimd
                def _(pool):
                    with loop(pool, 29, [(U["pool"], 2), (CH["pool"], 2)]):
                        for s in range(2):
                            split_unit(pool)

                @block.scalar
                def _(act):
                    u = U["act"]
                    for x in (eab_done, hi_ready, silu_done):
                        act.sem_inc(x, 1)
                    act.wait_ge(cw_turned, 1)
                    act.activation(cw, A[0][:, 0:160], ACT.Copy).then_inc(dt_steps, 1)
                    act.wait_ge(cst[1], 64)
                    act_take(act, [lambda b: act.activation(dx[0:64, 0:NP_], b[0:64, 0:NP_], ACT.Identity,
                                                            bias=dtb[0:64, 0:1]),
                                   lambda b: act.activation(dx[0:64, NP_:T], b[0:64, 0:NS], ACT.Identity,
                                                            bias=dtb[0:64, 0:1])], units=2)
                    act.wait_ge(dense_free, HF["act"].value + 2)
                    act.activation(dw[0:64, :], dx[0:64, :], ACT.Abs).then_inc(dt_steps, 1)
                    act.wait_ge(dt_steps, 2)
                    act.activation(du[0:64, :], dw[0:64, :], ACT.Exp, scale=-1.0).then_inc(dt_steps, 1)
                    act.activation(ea[0:64, :], alog[0:64, :], ACT.Exp).then_inc(dt_steps, 1)
                    act.wait_ge(dt_dve, 1)
                    act.activation(dl[0:64, :], dw[0:64, :], ACT.Ln).then_inc(dt_steps, 1)
                    act.wait_ge(dt_pe, 3)
                    act.activation(acs_tok, A[2][:, 0:384].rearrange("p (c h) -> p c h", h=64), ACT.Copy)\
                        .then_inc(dt_steps, 1)
                    act.activation(acsf[0:64, 0:512], A[4][0:64, :], ACT.Copy).then_inc(dt_steps, 1)
                    act.activation(acsf[0:64, 512:T], A[5][0:64, 0:256], ACT.Copy).then_inc(dt_steps, 1)
                    act.wait_ge(dt_dve, 5)
                    act.activation(w_tok, w_tok, ACT.Exp).then_inc(dt_steps, 1)
                    act.activation(tot_tok, tot_tok, ACT.Exp).then_inc(dt_steps, 1)
                    act.wait_ge(dt_dve, 7)

                    def take_raw(k):
                        act_take(act, [
                            lambda b: act.activation(raw[:, k % 2, 2:2 + NP_], b[:, 0:NP_], ACT.Copy),
                            lambda b: act.activation(raw[:, k % 2, 4 + NP_:4 + T], b[:, 0:NS], ACT.Copy)])

                    def silu(g, k, m, dst):
                        act.wait_ge(conv_done, g * 6 + (k + 1))
                        settle(act)
                        for t0, t1 in SPAN:
                            o = t0 and 2
                            act.activation(dst[:, t0:t1], conv[:, t0 + o:t1 + o], ACT.Silu,
                                           bias=cw[:, bass.ds(m + 120, 1)]).then_inc(silu_done, 1)

                    def take_x(n, a):
                        act.wait_ge(x_turned, n + 1)
                        settle(act)
                        act.activation(xtok[:, a, 0:2, :], A[2][:, 0:NP_].rearrange("p (c f) -> p c f", f=P), ACT.Copy)
                        act.activation(xtok[:, a, 2:6, :], A[3][:, :].rearrange("p (c f) -> p c f", f=P), ACT.Copy)\
                            .then_inc(x_taken, 1)

                    def decays(n):
                        act.wait_ge(ab_landed, n * 16 + 16)
                        act.wait_ge(gated, n + 1)
                        settle(act)
                        for d in range(2):
                            for h in range(2):
                                i = act.activation(eab[H64[h], d, :], ab[H64[h], d, h, :], ACT.Exp)
                        i.then_inc(eab_done, 1)
                        for q, (c0, c1) in enumerate(PARTS):
                            act.wait_ge(seg_ready, n * 2 + (q + 2))
                            act.activation(seg[:, 0:c1 - c0, :, :], seg[:, 0:c1 - c0, :, :], ACT.Exp)\
                                .then_inc(exp_done, 1)

                    def take_z(n, a):
                        take_spans(act, z, ACT.Silu)

                    def high(n, a):
                        act.wait_ge(gated, n + 2)
                        settle(act)
                        act.activation(Mh[:, a, :], y, ACT.Copy, scale=cw[:, bass.ds(n + 144, 1)]).then_inc(hi_ready, 1)

                    with loop(act, 4, [(U["act"], 14), (HF["act"], 20), (HD["act"], 10)]) as g:
                        take_raw(0)
                        take_raw(1)
                        silu(g, 0, g + 16, bT)
                        take_raw(2)
                        silu(g, 1, g + 20, cT)
                        for p in range(2):
                            k = 2 + 2 * p
                            if p:
                                take_raw(k)
                            take_raw(k + 1)
                            silu(g, k, g * 4 + 2 * p, xs[:, 0, :])
                            take_x(g * 4 + 2 * p, 0)
                            silu(g, k + 1, g * 4 + (2 * p + 1), xs[:, 1, :])
                            for a in range(2):
                                n = g * 4 + (2 * p + a)
                                if a:
                                    take_x(n, 1)
                                decays(n)
                                take_z(n, a)
                                high(n, a)
                            u.next()
                            u.next()
                    act.wait_ge(summed, 1)
                    act.activation(sd, A[0][:, 0:NT], ACT.Sqrt, scale=1.0 / INNER, bias=eps[:, 0:1]).then_inc(rooted, 1)

                @block.vector
                def _(dve):
                    c = chain(dve, "dve")
                    for x in (seg_ready, gated, carried):
                        dve.sem_inc(x, 1)
                    dve.memset(raw, 0.0).then_inc(zeroed, 1)
                    c.add(dve.memset(acc[:, :, :], 0.0))
                    c.link(dve.memset(sqsum, 0.0))
                    for _ in range(2):
                        U["dve"].next()
                        HF["dve"].next()
                    x64 = slice(0, 64)
                    dve.wait_ge(dt_steps, 4)
                    dve.tensor_scalar(dw[x64, :], du[x64, :], 1.0, None, ALU.add).then_inc(dt_dve, 1)
                    dve.wait_ge(dt_dve, 1)
                    c.add(dve.scalar_tensor_tensor(du[x64, :], dw[x64, :], -1.0, du[x64, :], ALU.add, ALU.subtract))
                    c.link(dve.reciprocal(acsf[x64, :], dw[x64, :]))
                    c.link(dve.tensor_tensor(du[x64, :], du[x64, :], acsf[x64, :], ALU.mult))
                    dve.wait_ge(dt_steps, 5)
                    c.link(dve.tensor_tensor(dl[x64, :], dl[x64, :], du[x64, :], ALU.subtract))
                    dve.scalar_tensor_tensor(dtf[x64, :], dx[x64, :], 0.0, dl[x64, :], ALU.max, ALU.add)\
                        .then_inc(dt_dve, 1)
                    dve.wait_ge(dt_dve, 2)
                    dve.tensor_scalar(af[x64, :], dtf[x64, :], ea[x64, 0:1], -1.0, ALU.mult, ALU.mult)\
                        .then_inc(dt_dve, 1)
                    dve.wait_ge(dt_pe, 1)
                    c.add(dve.tensor_copy(dt_tok, A[0][:, 0:384].rearrange("p (c h) -> p c h", h=64)))
                    dve.tensor_copy(a_tok, A[1][:, 0:384].rearrange("p (c h) -> p c h", h=64)).then_inc(dt_dve, 1)
                    dve.wait_ge(dt_pe, 3)
                    dve.wait_ge(dt_steps, 6)
                    c.add(dve.tensor_copy(tot_tok, A[3][:, 0:384].rearrange("p (c h) -> p c h", h=64)))
                    dve.tensor_tensor(w_tok, A[3][:, 0:384].rearrange("p (c h) -> p c h", h=64), acs_tok,
                                      ALU.subtract).then_inc(dt_dve, 1)
                    dve.wait_ge(dt_steps, 10)
                    dve.tensor_tensor(w_tok, w_tok, dt_tok, ALU.mult).then_inc(dt_dve, 1)
                    dve.wait_ge(cst[2], 32)
                    dve.wait_ge(dt_dve, 6)
                    dve.sem_inc(dt_dve, 1)

                    def conv5(g, k, m):
                        HF["dve"].next()
                        HF["dve"].next()
                        dve.wait_ge(dense_free, HF["dve"].value + 2)
                        dve.wait_ge(silu_done, g * 12 + 2 * k + 1)
                        settle(dve)
                        x = raw[:, k % 2, :]
                        w = T + 2
                        c.link(dve.tensor_scalar(conv, x[:, 0:w], cw[:, bass.ds(m, 1)], None, ALU.mult))
                        for j in range(1, 5):
                            i = dve.scalar_tensor_tensor(conv, x[:, j:j + w], cw[:, bass.ds(m + 24 * j, 1)], conv,
                                                         ALU.mult, ALU.add)
                            if j < 4:
                                c.link(i)
                            else:
                                i.then_inc(conv_done, 1)

                    def group_bc(g):
                        dve.wait_ge(bc_done, g + 1)
                        for q, (c0, c1) in enumerate(PARTS):
                            b = A[q][:, 0:(c1 - c0) * P].rearrange("p (c l) -> p c l", l=P)
                            for m, dst in ((mask_u, cb_u), (mask_l, cb_l)):
                                c.add(dve.tensor_tensor(dst[:, c0:c1, :], b,
                                                        m[:, :].unsqueeze(1).broadcast_to([P, c1 - c0, P]), ALU.mult))
                        c.add(dve.tensor_copy(btok[:, 0:2, :], A[2][:, 0:NP_].rearrange("p (c l) -> p c l", l=P)))
                        dve.tensor_copy(btok[:, 2:6, :], A[3][:, :].rearrange("p (c l) -> p c l", l=P))\
                            .then_inc(bc_taken, 1)
                        dve.wait_ge(bc_taken, g + 1)
                        c.wait()

                    def weigh(n, a):
                        dve.wait_ge(x_taken, n + 1)
                        dve.wait_ge(states_done, n + 1)
                        settle(dve)
                        for d in range(2):
                            i = dve.tensor_tensor(
                                xw[:, d, :, :].rearrange("p c (h f) -> p c h f", h=2),
                                xtok[:, a, :, :].rearrange("p c (h f) -> p c h f", h=2),
                                w_tok[:, :, bass.ds(n * 2 + 32 * d, 2)].unsqueeze(3).broadcast_to([P, NT, 2, 64]),
                                ALU.mult)
                            if d:
                                i.then_inc(xw_ready, 1)
                            else:
                                c.add(i)

                    def decay(n):
                        dve.wait_ge(ab_landed, n * 16 + 16)
                        dve.wait_ge(diag_done, n + 1)
                        settle(dve)
                        for q, (c0, c1) in enumerate(PARTS):
                            nb = c1 - c0
                            s, t2, dd = seg[:, 0:nb], tmp2[:, 0:nb], dec[:, c0:c1]
                            shape = [P, nb, 2, P]

                            def tok(t, d):
                                return t[:, c0:c1, bass.ds(n * 2 + 32 * d, 2)].unsqueeze(3).broadcast_to(shape)

                            def row(d):
                                return ab[:, d, :, c0 * P:c1 * P].rearrange("p h (c l) -> p c h l", l=P)

                            def cbx(t):
                                return t[:, c0:c1, :].unsqueeze(2).broadcast_to(shape)

                            c.add(dve.tensor_tensor(s, row(0), tok(acs_tok, 0), ALU.subtract))
                            c.link(dve.tensor_tensor(t2, row(1), tok(acs_tok, 1), ALU.subtract))
                            dve.tensor_tensor(s, s, t2, ALU.min).then_inc(seg_ready, 1)
                            dve.wait_ge(seg_ready, n * 2 + (q + 2))
                            settle(dve)
                            c.add(dve.tensor_tensor(dd, cbx(cb_u), tok(dt_tok, 0), ALU.mult))
                            c.link(dve.tensor_tensor(t2, cbx(cb_l), tok(dt_tok, 1), ALU.mult))
                            c.link(dve.tensor_tensor(dd, dd, t2, ALU.add))
                            dve.wait_ge(exp_done, n * 2 + (q + 1))
                            i = dve.tensor_tensor(dd, dd, s, ALU.mult)
                            if q:
                                i.then_inc(dec_ready, 1)
                            else:
                                c.link(i)

                    def carry(n):
                        dve.wait_ge(states_done, n + 2)
                        dve.wait_ge(off_done, n + 1)
                        settle(dve)
                        f, b = A[2], A[3]
                        c.add(dve.tensor_copy(prev[:, 0, 0:2, :], f[:, 0:256].rearrange("p (s f) -> p s f", f=P)))
                        c.add(dve.tensor_copy(prev[:, 1, 0, :], b[:, 0:P]))
                        c.link(dve.tensor_copy(prev[:, 1, 3, :], b[:, 3 * P:4 * P]))
                        for fwd, bwd in (((2, 1, 3), (2, 3, 4)), ((3, 2, 4), (1, 2, 3))):
                            for d, (dst, src, ch) in enumerate((fwd, bwd)):
                                for h in range(2):
                                    i = dve.scalar_tensor_tensor(
                                        prev[:, d, dst, H64[h]], prev[:, d, src, H64[h]],
                                        tot_tok[:, ch, bass.ds(n * 2 + (32 * d + h), 1)],
                                        (f, b)[d][:, dst * P + 64 * h:dst * P + 64 * h + 64], ALU.mult, ALU.add)
                                    if d == 1 and h == 1:
                                        if dst == 1:
                                            i.then_inc(carried, 1)
                                        else:
                                            c.link(i)
                                    else:
                                        c.add(i)

                    def combine(n, a):
                        dve.wait_ge(diag_done, n + 2)
                        dve.wait_ge(hi_ready, n + 1)
                        settle(dve)
                        for q, (t0, t1) in enumerate(SPAN):
                            c.add(dve.scalar_tensor_tensor(y[:, t0:t1], xs[:, a, t0:t1], dcol[:, bass.ds(n, 1)],
                                                           A[q][:, 0:t1 - t0], ALU.mult, ALU.add))
                        dve.wait_ge(off_done, n + 2)
                        dve.wait_ge(eab_done, n + 2)
                        settle(dve)
                        for d, dst in enumerate((F_DST, B_DST)):
                            for s0, s1 in ((0, 1), (1, 4)):
                                i = dve.tensor_tensor(tmp[:, s0 * P:s1 * P], A[4 + d][:, s0 * P:s1 * P],
                                                      eab[:, d, dst[s0] * P:(dst[s1 - 1] + 1) * P], ALU.mult)
                                c.link(i) if s0 else c.add(i)
                            for s0, s1 in ((0, 1), (1, 4)):
                                yy = y[:, dst[s0] * P:(dst[s1 - 1] + 1) * P]
                                i = dve.tensor_tensor(yy, yy, tmp[:, s0 * P:s1 * P], ALU.add)
                                c.link(i) if s0 else c.add(i)
                        HF["dve"].next()
                        HF["dve"].next()
                        dve.wait_ge(dense_free, HF["dve"].value + 2)
                        dve.tensor_tensor(y, y, z, ALU.mult).then_inc(gated, 1)
                        dve.wait_ge(gated, n + 2)
                        settle(dve)
                        c.link(dve.tensor_tensor(tmp, y, y, ALU.mult))
                        c.add(dve.tensor_tensor(sqsum, sqsum, tmp, ALU.add))
                        dve.wait_ge(hi_ready, n + 2)
                        settle(dve)
                        i = dve.scalar_tensor_tensor(Ml[:, a, :], y, cw[:, bass.ds(n + 144, 1)],
                                                     Mh[:, a, :].bitcast(F32), ALU.mult, ALU.subtract)
                        if a:
                            i.then_inc(mix_ready, 1)
                        else:
                            c.link(i)

                    with loop(dve, 4, [(U["dve"], 14), (HF["dve"], 20), (OF["dve"], 24), (OD["dve"], 20),
                                       (CH["dve"], DVE_PER)]) as g:
                        conv5(g, 0, g + 16)
                        conv5(g, 1, g + 20)
                        conv5(g, 2, g * 4)
                        group_bc(g)
                        for p in range(2):
                            if p:
                                conv5(g, 4, g * 4 + 2)
                            conv5(g, 3 + 2 * p, g * 4 + (2 * p + 1))
                            for a in range(2):
                                n = g * 4 + (2 * p + a)
                                weigh(n, a)
                                decay(n)
                                carry(n)
                                combine(n, a)
                            for _ in range(4 if p else 6):
                                U["dve"].next()
                            dve_out(dve)
                    dve.wait_ge(rooted, 1)
                    c.link(dve.reciprocal(rssd[:, :], sd))

                @block.tensor
                def _(pe):
                    for x in (off_done, diag_done, states_done):
                        pe.sem_inc(x, 1)
                    pe.wait_ge(cst[0], 48)
                    pe.transpose(A[0][:, 0:120], stage[0:120, 0, :], ident[0:120, 0:120])
                    pe.transpose(A[0][:, 120:160], stage[0:40, 1, :], ident[0:40, 0:40]).then_inc(cw_turned, 1)
                    pe_dense(pe, units=2)
                    pe.wait_ge(dt_dve, 3)
                    pe.wait_ge(dt_steps, 1)
                    for b, x in ((0, dtf), (1, af)):
                        for ch in range(NT):
                            mm = pe.transpose(A[b][:, ch * 64:(ch + 1) * 64], x[0:64, ch * P:(ch + 1) * P],
                                              ident[0:64, 0:64])
                    mm.then_inc(dt_pe, 1)
                    pe.wait_ge(dt_dve, 4)
                    for ch in range(NT):
                        for d, m in enumerate((mask_u, mask_l)):
                            pe.matmul(A[2][:, ch * 64 + 32 * d:ch * 64 + 32 * d + 32], m[:, :],
                                      a_tok[:, ch, 32 * d:32 * d + 32], start=True, stop=True)
                        mm = pe.matmul(A[3][:, ch * 64:(ch + 1) * 64], ones[:, :], a_tok[:, ch, :], start=True, stop=True)
                    mm.then_inc(dt_pe, 1)
                    for ch in range(NT):
                        for d, m in enumerate((mask_u, mask_l)):
                            mm = pe.matmul(A[4 + ch // 4][32 * d:32 * d + 32, (ch % 4) * P:(ch % 4 + 1) * P],
                                           a_tok[:, ch, 32 * d:32 * d + 32], m[:, :], start=True, stop=True)
                    mm.then_inc(dt_pe, 1)
                    pe.wait_ge(dt_dve, 7)

                    def turn6(x, done):
                        for ch in range(NT):
                            mm = pe.transpose(A[2 + (ch > 1)][:, (ch % 2 if ch < 2 else ch - 2) * P:][:, 0:P],
                                              x[:, ch * P:(ch + 1) * P], ident[:, :])
                        if done is not None:
                            mm.then_inc(done, 1)

                    def group_bc(g):
                        pe.wait_ge(silu_done, g * 12 + 5)
                        pe.wait_ge(gated, g * 4 + 1)
                        settle(pe)
                        turn6(bT, None)
                        for ch in range(NT):
                            mm = pe.matmul(A[ch > 1][:, (ch % 2 if ch < 2 else ch - 2) * P:][:, 0:P],
                                           bT[:, ch * P:(ch + 1) * P], cT[:, ch * P:(ch + 1) * P], start=True, stop=True)
                        mm.then_inc(bc_done, 1)

                    def turn_x(g, n, k, a):
                        pe.wait_ge(silu_done, g * 12 + (2 * k + 3))
                        pe.wait_ge(bc_taken, g + 1)
                        pe.wait_ge(carried, n + 1)
                        settle(pe)
                        turn6(xs[:, a, :], x_turned)

                    def states(n):
                        pe.wait_ge(xw_ready, n + 1)
                        settle(pe)
                        for d, src in enumerate((F_SRC, B_SRC)):
                            for s in range(4):
                                mm = pe.matmul(A[2 + d][:, s * P:(s + 1) * P], btok[:, src[s], :],
                                               xw[:, d, src[s], :], start=True, stop=True)
                        mm.then_inc(states_done, 1)

                    def scan_out(n, a):
                        pe.wait_ge(carried, n + 2)
                        pe.wait_ge(out_added, OF["pe"].value + 2)
                        settle(pe)
                        for d, dst in enumerate((F_DST, B_DST)):
                            for s in range(4):
                                mm = pe.matmul(A[4 + d][:, s * P:(s + 1) * P], prev[:, d, s, :],
                                               cT[:, dst[s] * P:(dst[s] + 1) * P], start=True, stop=True)
                        mm.then_inc(off_done, 1)
                        pe.wait_ge(dec_ready, n + 1)
                        settle(pe)
                        for ch in range(NT):
                            for h in range(2):
                                mm = pe.matmul(A[ch > 1][H64[h], (ch % 2 if ch < 2 else ch - 2) * P:][:, 0:P],
                                               xtok[:, a, ch, H64[h]], dec[:, ch, h, :], start=True, stop=True)
                        mm.then_inc(diag_done, 1)

                    with loop(pe, 4, [(U["pe"], 14), (HF["pe"], 20), (HD["pe"], 10), (OF["pe"], 24), (OD["pe"], 20),
                                      (MX["pe"], 2)]) as g:
                        pe_dense(pe)
                        pe_dense(pe)
                        pe_dense(pe)
                        group_bc(g)
                        for p in range(2):
                            if p:
                                pe_dense(pe)
                            pe_dense(pe)
                            for a in range(2):
                                n = g * 4 + (2 * p + a)
                                turn_x(g, n, 2 + 2 * p + a, a)
                                states(n)
                                pe_dense(pe)
                                scan_out(n, a)
                                pe.wait_ge(gated, n + 2)
                            pe_out(pe)
                    pe.wait_ge(mix_ready, MX["pe"].value)
                    for i in range(NT):
                        mm = pe.matmul(A[0][:, i:i + 1], sqsum[:, i * P:(i + 1) * P], ones[:, 0:1], start=True, stop=True)
                    mm.then_inc(summed, 1)

        def attention_phase():
            w_in = na_w_in[0]
            r = Region()
            qF, kF, vF, z, y = (r(T) for _ in range(5))
            V_FROM = [NP_ + t for t in (0, 64, 128, 192, 320, 384)] + [0, 96, 128]
            vT = r(len(V_FROM), P)
            B = [(0, 0, 256, NP_ + 128, NP_ + 64, 0, 3), (0, 256, 256, NP_ + 256, NP_ + 192, 0, 4),
                 (1, 0, 192, NP_, NP_, 256, 2), (1, 192, 192, NP_ + 384, NP_ + 320, 448, 5),
                 (2, 0, 160, 0, 0, 640, 0), (2, 160, 160, 128, 96, 800, 1)]
            S_AT = [0, 256, 512, 704, 896, 1056]
            NSC, NM = 1216, 960
            PTS = [(0, 0, 128, 1), (0, 128, 128, 3), (1, 0, 128, 3), (1, 128, 128, 4),
                   (2, 0, 128, 0), (3, 64, 128, 5), (4, 0, 128, 6), (5, 32, 128, 8),
                   (2, 128, 64, 2), (3, 0, 64, 4), (4, 128, 32, 8), (5, 0, 32, 7)]
            mask, Bm = r(NM), r(2, NM)
            gs, gq = r(2, 2, 256), r(2, 2, 192)
            Sb = r(2, NSC)
            PT = r(2, 12, P)
            O = r(NT, P)
            nmx, nmax, sums, rinv = (r(NT, 2) for _ in range(4))
            (masked, bm_ready, scored, max_ready, prob_ready, p_turned, pT_ready, pv_done, o_ready, o_turned,
             v_turned, v_taken, gated, hi_ready) = (
                sem("n_" + x) for x in (
                    "masked", "bm_ready", "scored", "max_ready", "prob_ready", "p_turned", "pT_ready", "pv_done",
                    "o_ready", "o_turned", "v_turned", "v_taken", "gated", "hi_ready"))
            bias_landed = [sem("n_bias_landed0"), sem("n_bias_landed1")]
            ROWS = (4, 8)

            def steps(eng, counts, step, end):
                step(0, 0, False)
                step(1, 1, True)
                with loop(eng, PAIRS // 2 - 1, counts) as i:
                    for a in range(2):
                        step(i * 2 + (2 + a), a, True)
                end()

            with nc.Block() as block:
                @block.sync
                def _(sp):
                    def step(n, a, prev):
                        if not isinstance(n, int):
                            sp.wait_ge(bm_ready, n - 1)
                            settle(sp)
                        for h in range(2):
                            for t, g, cols, rows, w in ((gs_dram, gs, 16, 8, 256), (gp_dram, gq, 32, 4, 192)):
                                per = t.shape[2] * t.shape[3]
                                win = bass.AP(t.tensor, 0, [[cols * per, HEADS], [per, cols], [t.shape[3], rows], [1, w]])
                                sp.dma_start(g[:, a, h, :], win[bass.ds(n * 2 + h, 1), :, :, :])\
                                    .then_inc(bias_landed[a], 16)
                        for base in (N_V, N_Q):
                            load_f(sp, w_in, bass.ds(n * P + base, P))
                        load_f(sp, w_in, bass.ds(n * P + N_K, P))
                        load_f(sp, w_in, bass.ds(n * P, P))
                        if a == 0 and prev:
                            load_out(sp, 1, bass.ds(n * P - 256, 256))

                    steps(sp, [(U["sp"], 10)], step, lambda: load_out(sp, 1, slice(14 * P, 16 * P)))

                @block.gpsimd
                def _(pool):
                    c = chain(pool, "pool")
                    c.link(pool.memset(mask, 0.0))

                    def bound(c0, n, rows, base, col, part):
                        m = mask[:, c0:c0 + n * rows].rearrange("p (j r) -> p j r", r=rows)
                        c.link(pool.affine_select(out=m, in_=m, compare_op=ALU.is_ge, fill=NEG, base=base,
                                                  pattern=[[col, n], [0, rows]], channel_multiplier=part))

                    bound(0, 32, 8, 7, 8, -1)
                    bound(0, 32, 8, 120, -8, 1)
                    bound(256, 24, 8, 71, 8, -1)
                    bound(256 + 16 * 8, 8, 8, -72, -8, 1)
                    bound(448, 8, 8, 7, 8, -1)
                    bound(448, 24, 8, 120, -8, 1)
                    bound(640, 40, 4, 35, 4, -1)
                    bound(640 + 16 * 4, 24, 4, -36, -4, 1)
                    bound(800, 24, 4, 3, 4, -1)
                    bound(800, 40, 4, 60, -4, 1)

                    def biases(n, a, prev):
                        pool.wait_ge(bias_landed[a], (n - a) * 32 + 64)
                        if prev:
                            pool.wait_ge(max_ready, n * 2)
                        settle(pool)
                        for h in range(2):
                            for g, c0, c1, j0, rows in ((gs, 0, 256, 0, 8), (gs, 256, 448, 8, 8), (gs, 448, 640, 0, 8),
                                                        (gq, 640, 800, 8, 4), (gq, 800, 960, 0, 4)):
                                m, o = (x[:, c0:c1].rearrange("p (j r) -> p j r", r=rows) for x in (mask, Bm[:, h, :]))
                                src = g[:, a, h, :].rearrange("p (r j) -> p j r", r=rows)[
                                    :, j0:j0 + (c1 - c0) // rows, ::-1]
                                i = pool.tensor_tensor(o, m, src, ALU.add)
                        i.then_inc(bm_ready, 1)

                    def step(n, a, prev):
                        split_unit(pool)
                        split_unit(pool)
                        biases(n, a, prev)
                        for _ in range(4 if a == 0 and prev else 2):
                            split_unit(pool)

                    def end():
                        split_unit(pool)
                        split_unit(pool)

                    steps(pool, [(U["pool"], 10), (CH["pool"], 10)], step, end)

                @block.scalar
                def _(act):
                    def probs(n):
                        for h in range(2):
                            act.wait_ge(max_ready, n * 2 + (h + 1))
                            settle(act)
                            for b, (_, _, w, _, _, _, o) in enumerate(B):
                                s = Sb[:, h, S_AT[b]:S_AT[b] + w]
                                i = act.activation(s, s, ACT.Exp, bias=nmax[:, o, h:h + 1],
                                                   accum_out=sums[:, o, h:h + 1])
                            i.then_inc(prob_ready, 1)

                    def take_pt(n):
                        for h in range(2):
                            act.wait_ge(p_turned, n * 2 + (h + 1))
                            settle(act)
                            bk = A[3 * h:3 * h + 3]
                            act.activation(PT[:, h, 0:4, :], bk[0][:, :].rearrange("p (j q) -> p j q", q=P), ACT.Copy)
                            act.activation(PT[:, h, 4:8, :], bk[1][:, :].rearrange("p (j q) -> p j q", q=P), ACT.Copy)
                            act.activation(PT[0:64, h, 8:10, :],
                                           bk[2][0:64, 0:256].rearrange("p (j q) -> p j q", q=P), ACT.Copy)
                            act.activation(PT[0:32, h, 10:12, :],
                                           bk[2][0:32, 256:512].rearrange("p (j q) -> p j q", q=P), ACT.Copy)\
                                .then_inc(pT_ready, 1)

                    def take_vt(n):
                        act.wait_ge(v_turned, n + 1)
                        settle(act)
                        act.activation(vT[:, 0:4, :], A[2][:, :].rearrange("p (j f) -> p j f", f=P), ACT.Copy)
                        act.activation(vT[:, 4:8, :], A[3][:, :].rearrange("p (j f) -> p j f", f=P), ACT.Copy)
                        act.activation(vT[:, 8, :], A[4][:, 0:P], ACT.Copy).then_inc(v_taken, 1)

                    def high(n, a):
                        act.wait_ge(gated, n + 1)
                        settle(act)
                        act.activation(Mh[:, a, :], y, ACT.Copy).then_inc(hi_ready, 1)

                    def step(n, a, prev):
                        take_spans(act, vF)
                        if prev:
                            take_pt(n - 1)
                        take_spans(act, qF, scale=1.0 / 8)
                        take_vt(n)
                        take_spans(act, kF)
                        if prev:
                            high(n - 1, 1 - a)
                        take_spans(act, z, ACT.Silu)
                        if a == 0 and prev:
                            U["act"].next()
                            U["act"].next()
                        probs(n)

                    def end():
                        take_pt(15)
                        high(15, 1)
                        U["act"].next()
                        U["act"].next()

                    steps(act, [(U["act"], 10), (HF["act"], 16), (HD["act"], 8)], step, end)

                @block.vector
                def _(dve):
                    c = chain(dve, "dve")

                    def finish(n, a):
                        dve.wait_ge(prob_ready, n * 2 + 2)
                        settle(dve)
                        c.link(dve.reciprocal(rinv, sums))
                        dve.wait_ge(pv_done, n + 1)
                        settle(dve)
                        for t0, t1, bk in ((2, 6, 0), (0, 2, 1)):
                            i = dve.tensor_tensor(O[:, t0:t1, :].rearrange("p t (h f) -> p t h f", h=2),
                                                  A[bk][:, 0:(t1 - t0) * P].rearrange("p (t h f) -> p t h f", h=2, f=64),
                                                  rinv[:, t0:t1, :].unsqueeze(3).broadcast_to([P, t1 - t0, 2, 64]),
                                                  ALU.mult)
                        i.then_inc(o_ready, 1)
                        dve.wait_ge(o_turned, n + 1)
                        dve.wait_ge(dense_free, n * 8 + (Z0 + 8))
                        settle(dve)
                        for q, (t0, t1) in enumerate(SPAN):
                            rows = ROWS[q]
                            i = dve.tensor_tensor(y[:, t0:t1].rearrange("p (r c) -> p c r", r=rows),
                                                  A[5 - q][:, 0:t1 - t0].rearrange("p (c r) -> p c r", r=rows),
                                                  z[:, t0:t1].rearrange("p (c r) -> p c r", r=rows), ALU.mult)
                        i.then_inc(gated, 1)
                        dve.wait_ge(hi_ready, n + 1)
                        settle(dve)
                        i = dve.tensor_tensor(Ml[:, a, :], y, Mh[:, a, :].bitcast(F32), ALU.subtract)
                        if a:
                            i.then_inc(mix_ready, 1)
                        else:
                            c.link(i)

                    def scores(n):
                        dve.wait_ge(bm_ready, n + 1)
                        for h in range(2):
                            dve.wait_ge(scored, n * 2 + (h + 1))
                            settle(dve)
                            for b, (bk, c0, w, _, _, m, o) in enumerate(B):
                                i = dve.tensor_tensor_reduce(
                                    Sb[:, h, S_AT[b]:S_AT[b] + w], A[3 * h + bk][:, c0:c0 + w], Bm[:, h, m:m + w],
                                    1.0, -3e38, ALU.add, ALU.max, nmx[:, o, h:h + 1])
                                if b < len(B) - 1:
                                    c.add(i)
                            c.link(i)
                            dve.tensor_scalar(nmax[:, :, h], nmx[:, :, h], -1.0, None, ALU.mult)\
                                .then_inc(max_ready, 1)

                    Z0 = HF["dve"].value + 2

                    def step(n, a, prev):
                        if prev:
                            finish(n - 1, 1 - a)
                        for _ in range(4):
                            U["dve"].next()
                        for _ in range(8):
                            HF["dve"].next()
                        if a == 0 and prev:
                            dve_out(dve)
                        scores(n)

                    def end():
                        finish(15, 1)
                        dve_out(dve)

                    steps(dve, [(U["dve"], 10), (HF["dve"], 16), (OF["dve"], 12), (OD["dve"], 10),
                                (CH["dve"], 2 * (1 + 12) + 1)], step, end)

                @block.tensor
                def _(pe):
                    def turn_v():
                        pe.wait_ge(dense_free, HF["pe"].value)
                        for j, t in enumerate(V_FROM):
                            mm = pe.transpose(A[2 + j // 4][:, (j % 4) * P:(j % 4 + 1) * P], vF[:, t:t + P], ident[:, :])
                        mm.then_inc(v_turned, 1)

                    def score(n):
                        pe.wait_ge(dense_free, HF["pe"].value)
                        pe.wait_ge(v_taken, n + 1)
                        for h in range(2):
                            if h:
                                pe.wait_ge(out_added, OF["pe"].value + 2)
                            f = slice(64 * h, 64 * h + 64)
                            for bk, c0, w, q0, k0, _, _ in B:
                                mm = pe.matmul(A[3 * h + bk][:, c0:c0 + w], qF[f, q0:q0 + P], kF[f, k0:k0 + w],
                                               start=True, stop=True)
                            mm.then_inc(scored, 1)

                    def turn_p(n):
                        for h in range(2):
                            pe.wait_ge(prob_ready, n * 2 + (h + 1))
                            for j, (b, k0, w, _) in enumerate(PTS):
                                at = S_AT[b] + k0
                                mm = pe.transpose(A[3 * h + j // 4][0:w, (j % 4) * P:(j % 4 + 1) * P],
                                                  Sb[:, h, at:at + w], ident[:, :])
                            mm.then_inc(p_turned, 1)

                    def apply_v(n):
                        pe.wait_ge(pT_ready, n * 2 + 2)
                        for b, blk in enumerate(B):
                            o = blk[6]
                            bk, c0 = (0, (o - 2) * P) if o >= 2 else (1, o * P)
                            js = [j for j in range(12) if PTS[j][0] == b]
                            for h in range(2):
                                for j in js:
                                    w, t = PTS[j][2:]
                                    mm = pe.matmul(A[bk][:, c0 + 64 * h:c0 + 64 * h + 64], PT[0:w, h, j, :],
                                                   vT[0:w, t, 64 * h:64 * h + 64], start=(j == js[0]), stop=(j == js[1]))
                        mm.then_inc(pv_done, 1)

                    def turn_o(n):
                        pe.wait_ge(o_ready, n + 1)
                        for o in range(NT):
                            out = A[4][:, (o - 2) * P:(o - 1) * P] if o >= 2 else A[5][:, o * P:(o + 1) * P]
                            mm = pe.transpose(out, O[:, o, :], ident[:, :])
                        mm.then_inc(o_turned, 1)

                    def step(n, a, prev):
                        pe_dense(pe)
                        if prev:
                            turn_p(n - 1)
                        pe_dense(pe)
                        if prev:
                            apply_v(n - 1)
                        turn_v()
                        pe_dense(pe)
                        if prev:
                            pe.wait_ge(v_taken, n + 1)
                            turn_o(n - 1)
                        pe_dense(pe)
                        if prev:
                            if a == 0:
                                pe_out(pe)
                            pe.wait_ge(gated, n)
                        score(n)

                    def end():
                        turn_p(15)
                        apply_v(15)
                        turn_o(15)
                        pe_out(pe)

                    steps(pe, [(U["pe"], 10), (HF["pe"], 16), (HD["pe"], 8), (OF["pe"], 12), (OD["pe"], 10),
                               (MX["pe"], 1)], step, end)

        def post_phase(L):
            r = Region()
            macc, res, gain, junk = r(NT, D), r(NT, D), r(D), r(D)
            ss, sd, rr = r(NT), r(NT), r(NT)
            n = f"p{L}_"
            landed, res_landed, summed, squared, rooted, done, stored = (
                sem(n + x) for x in ("landed", "res_landed", "summed", "squared", "rooted", "done", "stored"))
            with nc.Block() as block:
                @block.sync
                def _(sp):
                    sp.dma_start(gain, post_g[L:L + 1, :].broadcast_to([P, D])).then_inc(landed, 16)
                    if L == 0:
                        sp.dma_start(macc, macc_dram.rearrange("(i p) c -> p i c", p=P)).then_inc(landed, 16)
                        sp.dma_start(res[:, 0:2, :], x_prompt[0].rearrange("(i p) c -> p i c", p=P)).then_inc(res_landed, 16)
                        sp.dma_start(res[:, 2:6, :], x_sample[0].rearrange("(i p) c -> p i c", p=P)).then_inc(res_landed, 16)
                    else:
                        sp.dma_start(res, x1_dram.rearrange("(i p) c -> p i c", p=P)).then_inc(res_landed, 32)
                    for i in range(NT):
                        sp.wait_ge(done, i + 1)
                        if L == 0:
                            dst = x1_dram[i * P:(i + 1) * P, :]
                        elif i < 2:
                            dst = y_prompt[0, i * P:(i + 1) * P, :]
                        else:
                            dst = y_sample[0, (i - 2) * P:(i - 1) * P, :]
                        sp.dma_start(dst, acc[:, i, :]).then_inc(stored, 16)
                    sp.wait_ge(stored, 16 * NT)

                @block.vector
                def _(dve):
                    c = chain(dve, "dve")
                    if L == 0:
                        dve.wait_ge(landed, 32)
                        for i in range(NT):
                            dve.scalar_tensor_tensor(acc[:, i, :], acc[:, i, :], rssd[:, i:i + 1], macc[:, i, :],
                                                     ALU.mult, ALU.add).then_inc(summed, 1)
                    dve.wait_ge(landed, 16)
                    dve.wait_ge(rooted, 1)
                    c.link(dve.reciprocal(rr, sd))
                    dve.wait_ge(res_landed, 32)
                    for i in range(NT):
                        c.link(dve.scalar_tensor_tensor(acc[:, i, :], acc[:, i, :], rr[:, i:i + 1], gain,
                                                        ALU.mult, ALU.mult))
                        dve.tensor_tensor(acc[:, i, :], acc[:, i, :], res[:, i, :], ALU.add).then_inc(done, 1)

                @block.scalar
                def _(act):
                    for i in range(NT):
                        if L == 0:
                            act.wait_ge(summed, i + 1)
                        if i:
                            act.wait_ge(squared, i)
                        act.activation(junk, acc[:, i, :], ACT.Square, accum_out=ss[:, i:i + 1]).then_inc(squared, 1)
                    act.wait_ge(squared, NT)
                    act.activation(sd, ss, ACT.Sqrt, scale=1.0 / D, bias=eps[:, 0:1]).then_inc(rooted, 1)

        setup()
        memory_phase(0)
        ssd_phase()
        post_phase(0)
        memory_phase(1)
        attention_phase()
        post_phase(1)


_INS = ["x_prompt", "x_sample", "mem_prompt", "mem_sample", "pre_g", "post_g", "mem_g", "w_mem_kv", "w_out",
        "ssd_w_in", "ssd_conv_w", "ssd_conv_b", "ssd_dt_bias_f", "ssd_dt_bias_b", "ssd_a_log_f", "ssd_a_log_b",
        "ssd_d", "ssd_norm_g", "na_w_in", "na_rpb"]
_OUTS = [(1, NP_, D), (1, NS, D)]


def kernel(**inputs):
    import numpy as _np
    import concourse.bacc as _bacc
    from concourse.bass_utils import run_bass_kernel_spmd as _run

    nc = _bacc.Bacc("TRN2", target_bir_lowering=False, num_devices=1)
    arrays, args = {}, []
    for name in _INS:
        a = _np.ascontiguousarray(inputs[name])
        arrays[f"in_{name}_dram"] = a
        args.append(nc.dram_tensor(f"in_{name}_dram", a.shape, mybir.dt.from_np(a.dtype), kind="ExternalInput").ap())
    for i, shape in enumerate(_OUTS):
        args.append(nc.dram_tensor(f"out_{i}_dram", shape, F32, kind="ExternalOutput").ap())
    encoder_kernel(nc, *args)
    r = _run(nc, [arrays], core_ids=[0])
    return tuple(r.results[0][f"out_{i}_dram"] for i in range(len(_OUTS)))
```
